# Optimizing a Trainium2 kernel written in Bass

```python
import jax, jax.numpy as jnp
from jax import lax
import numpy as np

D_MODEL = 2048
BATCH = 1
SEQ = 256
DEPTH = 1

D_FF = 5632
CONV_WIDTH = 4
RG_WIDTH = 2048
RG_BLOCKS = 8
RG_BLOCK = RG_WIDTH // RG_BLOCKS
RG_C = 8.0
M_HEADS = 8
M_HEAD_DIM = 256
M_WIDTH = M_HEADS * M_HEAD_DIM
M_CHUNK = 128
NORM_EPS = 1e-6
IN_SIZES = (RG_WIDTH, RG_WIDTH, M_WIDTH, M_WIDTH, D_MODEL, D_MODEL, M_HEADS, M_HEADS)
D_IN = 2 * RG_WIDTH + 2 * M_WIDTH + 2 * D_MODEL + 2 * M_HEADS

kernel_name = 'hybrid_rglru_mlstm_macaron'

def rms_norm(x, g):
    x32 = x.astype(jnp.float32)
    y = x32 * lax.rsqrt(jnp.mean(x32 * x32, axis=-1, keepdims=True) + NORM_EPS)
    return (y * g.astype(jnp.float32)).astype(x.dtype)

def swiglu_ffn(u, w_gate, w_up, w_down):
    return (jax.nn.silu(u @ w_gate) * (u @ w_up)) @ w_down

def causal_depthwise_conv(x, w, b):
    k, c = w.shape
    y = lax.conv_general_dilated(x, w[:, None, :].astype(x.dtype), window_strides=(1,),
                                 padding=[(k - 1, 0)], dimension_numbers=('NWC', 'WIO', 'NWC'),
                                 feature_group_count=c)
    return y + b.astype(x.dtype)

def _linear_recurrence_combine(left, right):
    a_l, b_l = left
    a_r, b_r = right
    return a_l * a_r, a_r * b_l + b_r

def rglru_branch(u_x, u_gate, conv_w, conv_b, w_a, b_a, w_x, b_x, lam):
    bsz, s, _ = u_x.shape
    xc = causal_depthwise_conv(u_x, conv_w, conv_b).astype(jnp.float32)
    xb = xc.reshape(bsz, s, RG_BLOCKS, RG_BLOCK)
    r = jax.nn.sigmoid(jnp.einsum('bsnd,nde->bsne', xb, w_a.astype(jnp.float32)) + b_a.astype(jnp.float32))
    i = jax.nn.sigmoid(jnp.einsum('bsnd,nde->bsne', xb, w_x.astype(jnp.float32)) + b_x.astype(jnp.float32))
    r = r.reshape(bsz, s, RG_WIDTH)
    i = i.reshape(bsz, s, RG_WIDTH)
    log_a = -RG_C * r * jax.nn.softplus(-lam.astype(jnp.float32))
    a = jnp.exp(log_a)
    beta = jnp.sqrt(-jnp.expm1(2.0 * log_a)) * (i * xc)
    _, h = lax.associative_scan(_linear_recurrence_combine, (a, beta), axis=1)
    return h.astype(u_x.dtype) * jax.nn.gelu(u_gate)

def mlstm_chunkwise(q, k, v, log_i, log_f):
    bsz, nh, s, d = q.shape
    nc, L = s // M_CHUNK, M_CHUNK
    q = q.reshape(bsz, nh, nc, L, d)
    k = k.reshape(bsz, nh, nc, L, d)
    v = v.reshape(bsz, nh, nc, L, d)
    log_i = log_i.reshape(bsz, nh, nc, L)
    b = jnp.cumsum(log_f.reshape(bsz, nh, nc, L), axis=-1)
    g = b[..., -1]
    a = g[..., None] - b + log_i
    m_loc = jnp.max(a, axis=-1)
    w = jnp.exp(a - m_loc[..., None])
    c_loc = jnp.einsum('bhcl,bhclk,bhclv->bhckv', w, k, v)
    n_loc = jnp.einsum('bhcl,bhclk->bhck', w, k)

    def step(carry, inp):
        c_st, n_st, m_st = carry
        g_c, m_c, c_c, n_c = inp
        m_new = jnp.maximum(g_c + m_st, m_c)
        s_old = jnp.exp(g_c + m_st - m_new)
        s_loc = jnp.exp(m_c - m_new)
        c_new = s_old[..., None, None] * c_st + s_loc[..., None, None] * c_c
        n_new = s_old[..., None] * n_st + s_loc[..., None] * n_c
        return (c_new, n_new, m_new), (c_st, n_st, m_st)

    init = (jnp.zeros((bsz, nh, d, d), jnp.float32), jnp.zeros((bsz, nh, d), jnp.float32),
            jnp.zeros((bsz, nh), jnp.float32))
    xs = (jnp.moveaxis(g, 2, 0), jnp.moveaxis(m_loc, 2, 0), jnp.moveaxis(c_loc, 2, 0), jnp.moveaxis(n_loc, 2, 0))
    _, (c_prev, n_prev, m_prev) = lax.scan(step, init, xs)
    c_prev = jnp.moveaxis(c_prev, 0, 2)
    n_prev = jnp.moveaxis(n_prev, 0, 2)
    m_prev = jnp.moveaxis(m_prev, 0, 2)

    causal = jnp.tril(jnp.ones((L, L), dtype=bool))
    log_d = b[..., :, None] - b[..., None, :] + log_i[..., None, :]
    log_d = jnp.where(causal, log_d, -jnp.inf)
    log_inter = b + m_prev[..., None]
    m_t = jnp.maximum(log_inter, jnp.max(log_d, axis=-1))
    scores = jnp.einsum('bhctd,bhcsd->bhcts', q, k) * jnp.exp(log_d - m_t[..., None])
    inter_w = jnp.exp(log_inter - m_t)
    num = (jnp.einsum('bhcts,bhcsv->bhctv', scores, v)
           + inter_w[..., None] * jnp.einsum('bhctk,bhckv->bhctv', q, c_prev))
    den = jnp.sum(scores, axis=-1) + inter_w * jnp.einsum('bhctk,bhck->bhct', q, n_prev)
    h = num / jnp.maximum(jnp.abs(den), jnp.exp(-m_t))[..., None]
    return h.reshape(bsz, nh, s, d)

def head_layer_norm(h, g):
    mu = jnp.mean(h, axis=-1, keepdims=True)
    var = jnp.mean(jnp.square(h - mu), axis=-1, keepdims=True)
    y = (h - mu) * lax.rsqrt(var + NORM_EPS)
    return y.reshape(h.shape[0], h.shape[1], -1) * g.astype(jnp.float32)

def mlstm_branch(u_x, u_o, pre_i, pre_f, conv_w, conv_b, w_q, w_k, w_v, b_i, b_f, norm_g, skip):
    bsz, s, _ = u_x.shape
    xc = jax.nn.silu(causal_depthwise_conv(u_x, conv_w, conv_b))
    xch = xc.reshape(bsz, s, M_HEADS, M_HEAD_DIM)
    uxh = u_x.reshape(bsz, s, M_HEADS, M_HEAD_DIM)
    q = jnp.einsum('bshd,hde->bhse', xch, w_q).astype(jnp.float32)
    k = jnp.einsum('bshd,hde->bhse', xch, w_k).astype(jnp.float32) * (M_HEAD_DIM ** -0.5)
    v = jnp.einsum('bshd,hde->bhse', uxh, w_v).astype(jnp.float32)
    log_i = jnp.swapaxes((pre_i + b_i).astype(jnp.float32), 1, 2)
    log_f = jnp.swapaxes(jax.nn.log_sigmoid((pre_f + b_f).astype(jnp.float32)), 1, 2)
    h = mlstm_chunkwise(q, k, v, log_i, log_f)
    h = head_layer_norm(jnp.swapaxes(h, 1, 2), norm_g)
    h = h + skip.astype(jnp.float32) * xc.astype(jnp.float32)
    return (jax.nn.sigmoid(u_o.astype(jnp.float32)) * h).astype(u_x.dtype)

def hybrid_mixer(u, w_in, rg_conv_w, rg_conv_b, rg_w_a, rg_b_a, rg_w_x, rg_b_x, rg_lambda,
                 m_conv_w, m_conv_b, m_w_q, m_w_k, m_w_v, m_b_i, m_b_f, m_norm, m_skip,
                 w_proj_rg, w_proj_m, w_out):
    proj = u @ w_in
    offsets = []
    acc = 0
    for size in IN_SIZES[:-1]:
        acc += size
        offsets.append(acc)
    rg_x, rg_gate, m_x, m_o, gate_rg, gate_m, m_i, m_f = jnp.split(proj, offsets, axis=-1)
    y_rg = rglru_branch(rg_x, rg_gate, rg_conv_w, rg_conv_b, rg_w_a, rg_b_a, rg_w_x, rg_b_x, rg_lambda)
    y_m = mlstm_branch(m_x, m_o, m_i, m_f, m_conv_w, m_conv_b, m_w_q, m_w_k, m_w_v, m_b_i, m_b_f, m_norm, m_skip)
    merged = jax.nn.sigmoid(gate_rg) * (y_rg @ w_proj_rg) + jax.nn.sigmoid(gate_m) * (y_m @ w_proj_m)
    return merged @ w_out

def setup_inputs(seed: int = 0) -> dict:
    key = jax.random.key(seed)
    ks = iter(jax.random.split(key, 40))
    f32 = jnp.float32

    def nrm(shape, scale):
        return jax.random.normal(next(ks), shape, f32) * scale

    L = DEPTH
    x = nrm((BATCH, SEQ, D_MODEL), 1.0)
    ffn1_norm = 1.0 + nrm((L, D_MODEL), 0.1)
    ffn1_w_gate = nrm((L, D_MODEL, D_FF), D_MODEL ** -0.5)
    ffn1_w_up = nrm((L, D_MODEL, D_FF), D_MODEL ** -0.5)
    ffn1_w_down = nrm((L, D_FF, D_MODEL), D_FF ** -0.5)
    mix_norm = 1.0 + nrm((L, D_MODEL), 0.1)
    w_in = nrm((L, D_MODEL, D_IN), D_MODEL ** -0.5)
    rg_conv_w = nrm((L, CONV_WIDTH, RG_WIDTH), CONV_WIDTH ** -0.5)
    rg_conv_b = nrm((L, RG_WIDTH), 0.01)
    rg_w_a = nrm((L, RG_BLOCKS, RG_BLOCK, RG_BLOCK), RG_BLOCK ** -0.5)
    rg_b_a = nrm((L, RG_BLOCKS, RG_BLOCK), 0.01)
    rg_w_x = nrm((L, RG_BLOCKS, RG_BLOCK, RG_BLOCK), RG_BLOCK ** -0.5)
    rg_b_x = nrm((L, RG_BLOCKS, RG_BLOCK), 0.01)
    a_base = jax.random.uniform(next(ks), (L, RG_WIDTH), f32, minval=0.9, maxval=0.999)
    rg_lambda = jnp.log(a_base) - jnp.log1p(-a_base)
    m_conv_w = nrm((L, CONV_WIDTH, M_WIDTH), CONV_WIDTH ** -0.5)
    m_conv_b = nrm((L, M_WIDTH), 0.01)
    m_w_q = nrm((L, M_HEADS, M_HEAD_DIM, M_HEAD_DIM), M_HEAD_DIM ** -0.5)
    m_w_k = nrm((L, M_HEADS, M_HEAD_DIM, M_HEAD_DIM), M_HEAD_DIM ** -0.5)
    m_w_v = nrm((L, M_HEADS, M_HEAD_DIM, M_HEAD_DIM), M_HEAD_DIM ** -0.5)
    m_b_i = nrm((L, M_HEADS), 0.1)
    m_b_f = jnp.linspace(3.0, 6.0, M_HEADS, dtype=f32)[None, :] + nrm((L, M_HEADS), 0.1)
    m_norm = 1.0 + nrm((L, M_WIDTH), 0.1)
    m_skip = 1.0 + nrm((L, M_WIDTH), 0.1)
    w_proj_rg = nrm((L, RG_WIDTH, D_MODEL), RG_WIDTH ** -0.5)
    w_proj_m = nrm((L, M_WIDTH, D_MODEL), M_WIDTH ** -0.5)
    w_out = nrm((L, D_MODEL, D_MODEL), D_MODEL ** -0.5)
    ffn2_norm = 1.0 + nrm((L, D_MODEL), 0.1)
    ffn2_w_gate = nrm((L, D_MODEL, D_FF), D_MODEL ** -0.5)
    ffn2_w_up = nrm((L, D_MODEL, D_FF), D_MODEL ** -0.5)
    ffn2_w_down = nrm((L, D_FF, D_MODEL), D_FF ** -0.5)
    final_norm = 1.0 + nrm((D_MODEL,), 0.1)
    return {'x': x, 'ffn1_norm': ffn1_norm, 'ffn1_w_gate': ffn1_w_gate, 'ffn1_w_up': ffn1_w_up,
            'ffn1_w_down': ffn1_w_down, 'mix_norm': mix_norm, 'w_in': w_in,
            'rg_conv_w': rg_conv_w, 'rg_conv_b': rg_conv_b, 'rg_w_a': rg_w_a, 'rg_b_a': rg_b_a,
            'rg_w_x': rg_w_x, 'rg_b_x': rg_b_x, 'rg_lambda': rg_lambda,
            'm_conv_w': m_conv_w, 'm_conv_b': m_conv_b, 'm_w_q': m_w_q, 'm_w_k': m_w_k, 'm_w_v': m_w_v,
            'm_b_i': m_b_i, 'm_b_f': m_b_f, 'm_norm': m_norm, 'm_skip': m_skip,
            'w_proj_rg': w_proj_rg, 'w_proj_m': w_proj_m, 'w_out': w_out,
            'ffn2_norm': ffn2_norm, 'ffn2_w_gate': ffn2_w_gate, 'ffn2_w_up': ffn2_w_up,
            'ffn2_w_down': ffn2_w_down, 'final_norm': final_norm}

def reference(x, ffn1_norm, ffn1_w_gate, ffn1_w_up, ffn1_w_down, mix_norm, w_in,
              rg_conv_w, rg_conv_b, rg_w_a, rg_b_a, rg_w_x, rg_b_x, rg_lambda,
              m_conv_w, m_conv_b, m_w_q, m_w_k, m_w_v, m_b_i, m_b_f, m_norm, m_skip,
              w_proj_rg, w_proj_m, w_out, ffn2_norm, ffn2_w_gate, ffn2_w_up, ffn2_w_down, final_norm):
    h = x
    for l in range(DEPTH):
        h = h + 0.5 * swiglu_ffn(rms_norm(h, ffn1_norm[l]), ffn1_w_gate[l], ffn1_w_up[l], ffn1_w_down[l])
        h = h + hybrid_mixer(rms_norm(h, mix_norm[l]), w_in[l],
                             rg_conv_w[l], rg_conv_b[l], rg_w_a[l], rg_b_a[l], rg_w_x[l], rg_b_x[l], rg_lambda[l],
                             m_conv_w[l], m_conv_b[l], m_w_q[l], m_w_k[l], m_w_v[l], m_b_i[l], m_b_f[l],
                             m_norm[l], m_skip[l], w_proj_rg[l], w_proj_m[l], w_out[l])
        h = h + 0.5 * swiglu_ffn(rms_norm(h, ffn2_norm[l]), ffn2_w_gate[l], ffn2_w_up[l], ffn2_w_down[l])
    return rms_norm(h, final_norm)


_drawn_inputs = setup_inputs


def setup_inputs(seed=0):
    import zlib

    import numpy as np

    out = dict(_drawn_inputs(seed))
    spreads = {}
    factors = {'rg_conv_b': 8.0,
     'rg_b_a': 64.0,
     'rg_b_x': 64.0,
     'm_conv_b': 8.0,
     'm_b_i': 64.0,
     'm_skip': 3.356}
    for name, (base, spread) in spreads.items():
        noise = np.random.default_rng([zlib.crc32(name.encode()), seed]).standard_normal(out[name].shape)
        drawn = base * np.exp(spread * noise) if base else spread * noise
        out[name] = __import__('jax').numpy.asarray(drawn.astype(out[name].dtype))
    for name, factor in factors.items():
        out[name] = (out[name] * factor).astype(out[name].dtype)
    return out
```

```python
def hybrid_block(nc, ins, out):
    import concourse.bass as bass
    from concourse import mybir
    from contextlib import ExitStack

    f32, f32r = mybir.dt.float32, mybir.dt.float32r
    ALU = mybir.AluOpType
    ACT = mybir.ActivationFunctionType
    AX = mybir.AxisListType.X
    ds = bass.ds

    P = 128
    SEQ, DM = ins["x"].shape[1:]
    DFF = ins["ffn1_w_gate"].shape[2]
    HALVES = SEQ // P
    KT = DM // P
    FT = DFF // P
    NB = 512
    DB = DM // NB
    FB = DFF // NB
    TPB = NB // P
    HEADS = ins["m_b_i"].shape[1]
    HD = DM // HEADS
    CW = ins["rg_conv_w"].shape[1]
    EPS = 1e-6
    RG_C = 8.0
    RING = 4
    COL = {"rg_x": 0, "rg_gate": DM, "m_x": 2 * DM, "m_o": 3 * DM, "gate_rg": 4 * DM, "gate_m": 5 * DM,
           "if": 6 * DM}
    GU = 16
    DN = FT // 2
    MX = 32
    PJ = 16
    S_FFN1 = 0
    S_DN1 = S_FFN1 + GU * FB
    S_MIX = S_DN1 + DN * DB
    S_PRG = S_MIX + MX * DB
    S_PM = S_PRG + PJ * DB
    S_WO = S_PM + PJ * DB
    S_FFN2 = S_WO + 8 * DB
    S_DN2 = S_FFN2 + GU * FB
    AB = {"ffn1": 0, "dn1": FB, "mix": FB + 2, "prg": FB + 10, "pm": FB + 14, "wo": FB + 18,
          "ffn2": FB + 20, "dn2": 2 * FB + 20}
    C_FFN1 = 4
    C_DN1 = C_FFN1 + FB
    C_MIX = C_DN1 + DB
    C_PM = C_MIX + 8 * DB
    C_WO = C_PM + DB
    C_FFN2 = C_WO + DB
    D_PREP = 2
    N_PREP = 5
    D_MIX = D_PREP + N_PREP

    with ExitStack() as ctx:
        at = [256]

        def put(name, shape, dt, offset=None):
            size = 4
            for d in shape[1:]:
                size *= d
            size = (size + 31) // 32 * 32
            if offset is None:
                offset = at[0]
                at[0] += size
            return nc.alloc_sbuf_tensor_at(name, shape, dt, offset=offset), offset

        w_raw, _ = put("w_raw", [P, RING, 2, NB], f32)
        w_hi, _ = put("w_hi", [P, RING, 2, NB], f32r)
        w_lo, _ = put("w_lo", [P, RING, 2, NB], f32r)
        h, _ = put("h", [P, HALVES, DM], f32)
        uT_hi, o_u = put("uT_hi", [P, KT, SEQ], f32r)
        uT_lo, _ = put("uT_lo", [P, KT, SEQ], f32r)
        tok, _ = put("tok", [P, HALVES, NB], f32)
        sg, o_sg = put("sg", [P, HALVES, NB], f32)
        region = at[0]
        hid_hi, _ = put("hid_hi", [P, FT, SEQ], f32r)
        hid_lo, _ = put("hid_lo", [P, FT, SEQ], f32r)
        KB16 = KT * SEQ * 4
        yr_hi, _ = put("yr_hi", [P, KT, SEQ], f32r, region)
        yr_lo, _ = put("yr_lo", [P, KT, SEQ], f32r, region + KB16)
        ym_hi, _ = put("ym_hi", [P, KT, SEQ], f32r, region + 2 * KB16)
        ym_lo, _ = put("ym_lo", [P, KT, SEQ], f32r, region + 3 * KB16)
        mg_hi, _ = put("mg_hi", [P, KT, SEQ], f32r, region)
        mg_lo, _ = put("mg_lo", [P, KT, SEQ], f32r, region + KB16)
        ECOL = SEQ + P
        decay, _ = put("decay", [P, HEADS, ECOL], f32, region + 4 * KB16)
        o_wts = region + 4 * KB16 + HEADS * ECOL * 4
        w_heads, _ = put("w_heads", [P, 3, 4, HD], f32, o_wts)
        merged, _ = put("merged", [P, HALVES, DM], f32, region + 4 * KB16)
        vraw, _ = put("vraw", [P, 4, P], f32, region)
        VROWS = (KT, 7 * KT, 2 * CW * KT, 2 * KT)
        gfin, _ = put("gfin", [P, DM], f32, o_u)
        PAD = CW - 1
        xT, _ = put("xT", [P, TPB, PAD + SEQ], f32)
        xc, o_xc = put("xc", [P, TPB, SEQ], f32)
        b2, o_b2 = put("b2", [P, TPB, SEQ], f32)
        vtok, o_b3 = put("vtok", [P, HALVES, 2, HD + 2], f32)
        b5, o_b5 = put("b5", [P, TPB, SEQ], f32)
        b6, o_b6 = put("b6", [P, TPB, SEQ], f32)
        b3 = put("b3", [P, TPB, SEQ], f32, o_b3)[0]
        b4 = put("b4", [P, TPB, SEQ], f32, o_sg)[0]
        b4tok = put("b4tok", [P, HALVES, NB], f32, o_sg)[0]
        sdec = put("sdec", [P, 2, ECOL], f32, o_b6)[0]
        wif_raw = put("wif_raw", [P, KT, 2 * HEADS], f32, o_b3)[0]
        wif_hi = put("wif_hi", [P, KT, 2 * HEADS], f32r, o_xc)[0]
        wif_lo = put("wif_lo", [P, KT, 2 * HEADS], f32r, o_xc + KT * 2 * HEADS * 4)[0]
        sel = put("sel", [HEADS, HEADS, P], f32, o_b2)[0]
        hr = put("hr", [HEADS, 4, SEQ], f32, o_b6)[0]
        hs = put("hs", [HEADS, 4, SEQ], f32, o_b5)[0]
        V = {n: i for i, n in enumerate(
            ["ffn1_norm", "mix_norm", "ffn2_norm", "rg_lambda", "rg_b_a", "rg_b_x", "rg_conv_b", "m_conv_b"])}
        V["rg_conv_w"], V["m_conv_w"], V["m_norm"], V["m_skip"] = 8, 8 + CW, 8 + 2 * CW, 9 + 2 * CW
        NV = 10 + 2 * CW
        vec, _ = put("vec", [P, NV, KT], f32)
        cur, _ = put("cur", [P, NV, TPB], f32)
        ident, _ = put("ident", [P, P], f32)
        gtok, _ = put("gtok", [P, HALVES, 2 * HEADS], f32)
        colc, _ = put("colc", [P, HALVES, HEADS], f32)
        cole, _ = put("cole", [P, HALVES, HEADS], f32)
        bif, _ = put("bif", [HEADS, 2], f32)
        eps, _ = put("eps", [P, 1], f32)
        ssq, _ = put("ssq", [P, 4, HALVES, DB], f32)
        ms, _ = put("ms", [P, 4, HALVES], f32)
        junk, _ = put("junk", [P, NB], f32)
        rstd, _ = put("rstd", [P, 4, HALVES], f32)
        small, _ = put("small", [P, 8, 4], f32)
        bn, _ = put("bn", [P, 4, 6], f32)
        mv, _ = put("mv", [P, 4, 2], f32)
        spl, _ = put("spl", [P, 3, KT], f32)
        assert at[0] <= 229344, at[0]

        ps = [ctx.enter_context(nc.psum_tensor(f"bank{b}", [P, NB], f32)) for b in range(8)]
        PAIR = {"A": (0, 1), "B": (2, 3), "C": (4, 5), "D": (6, 7)}

        def sem(name):
            return ctx.enter_context(nc.semaphore(name))

        w_loaded = [sem(f"w_loaded{r}") for r in range(RING)]
        hi_ready, lo_ready, slot_used = sem("hi_ready"), sem("lo_ready"), sem("slot_used")
        mm = {p: sem(f"mm_{p}") for p in "CD"}
        ev = {p: sem(f"ev_{p}") for p in PAIR}
        split_hi = sem("split_hi")
        part_loaded = [sem(f"part_loaded{q}") for q in range(4)]
        x_loaded = [sem(f"x_loaded{q}") for q in range(DB)]
        misc_loaded = sem("misc_loaded")
        gfin_loaded = sem("gfin_loaded")
        qkv_loaded, ax_loaded = sem("qkv_loaded"), sem("ax_loaded")
        consts_ready, sel_ready = sem("consts_ready"), sem("sel_ready")
        lam_act = sem("lam_act")
        sq_ready, ssum_ready, root_ready, rstd_ready = (
            sem("sq_ready"), sem("ssum_ready"), sem("root_ready"), sem("rstd_ready"))
        dve_step, act_step, pool_step = sem("dve_step"), sem("act_step"), sem("pool_step")
        wif_hi_ready, wif_ready = sem("wif_hi_ready"), sem("wif_ready")
        prep = {n: sem(f"prep_{n}") for n in ("rows", "ln", "cols", "exp", "masked")}
        mx = {n: sem(f"mix_{n}") for n in (
            "conv_m", "silu", "var", "root", "ym_hi", "ym_lo", "conv_r", "at", "neg", "beta_root",
            "yr_hi", "yr_lo")}
        out_ready, out_done = sem("out_ready"), sem("out_done")
        lam_ready = sem("lam_ready")

        RES = {1: AB["dn1"], 2: AB["wo"], 3: AB["dn2"]}
        RES_SLOT = {1: (S_DN1, DN), 2: (S_WO, 8), 3: (S_DN2, DN)}
        SP = {"x": 0, "ffn1": DB, "dn1": DB + FB, "pm": 2 * DB + FB, "wo": 3 * DB + FB, "ffn2": 4 * DB + FB}

        X_USE = (("D", 0), ("C", 1), ("D", 1), ("C", 3))

        class Steps:

            def __init__(self, eng, s):
                self.eng, self.s, self.base, self.local = eng, s, 0, 0

            def then(self, ins):
                self.local += 1
                ins.then_inc(self.s, 1)
                self.eng.wait_ge(self.s, self.base + self.local)

            def loop(self, i, first, per):
                self.base0 = self.base + self.local
                self.base, self.local, self.per = self.base0 + (i - first) * per, 0, per

            def leave(self, turns):
                assert self.local == self.per, (self.local, self.per)
                self.base, self.local = self.base0 + turns * self.per, 0

        def wait(eng, s, v):
            if not isinstance(v, int) or v > 0:
                eng.wait_ge(s, v)

        def w_slot(src, rows, col, per_slot=2):
            return src[0, rows * P:(rows + 2) * P, ds(col, NB)].rearrange("(k p) c -> p k c", p=P)

        def slot(base, per, i, j):
            if isinstance(i, int):
                s = base + per * i + j
                return s, s % RING, s // RING + 1
            assert base % RING == 0 and per % RING == 0
            return base + j + per * i, j % RING, base // RING + j // RING + 1 + i * (per // RING)

        block = ctx.enter_context(nc.Block())

        @block.sync
        def _(sp):
            def load(base, per, i, j, src, row_tile, col, first=0):
                s, r, _ = slot(base - first * per, per, i, j)
                col = i * NB + (col - first * NB)
                wait(sp, lo_ready, s - RING + 1)
                sp.dma_start(w_raw[:, r, :, :], w_slot(src, row_tile, col)).then_inc(w_loaded[r], 16)

            def ffn_loads(base, gate, up, down, last=False):
                def body(i, start=0):
                    for j in range(start, GU):
                        load(base, GU, i, j, gate if j < 8 else up, 2 * (j % 8), 0)
                body(0, 0 if base else RING)
                with sp.Fori(1, FB) as i:
                    body(i)
                for q in range(DB):
                    for j in range(DN):
                        load(base + GU * FB, DN, q, j, down, 2 * j, 0)
                    if last and q == 1:
                        sp.wait_ge(slot_used, S_DN2)
                        sp.dma_start(gfin[:, :], ins["final_norm"].rearrange("(a d) -> a d", a=1)
                                     .to_broadcast([P, DM])).then_inc(gfin_loaded, 16)

            def rows_of(name):
                x = ins[name]
                return x.rearrange("a (k p) -> (a k) p", p=P) if len(x.shape) == 2 else \
                    x.rearrange("a b (k p) -> (a b k) p", p=P)

            for q in range(DB):
                sp.dma_start(h[:, :, q * NB:(q + 1) * NB],
                             ins["x"][0].rearrange("(t p) d -> p t d", p=P)[:, :, q * NB:(q + 1) * NB])\
                    .then_inc(x_loaded[q], 16)
                load(S_FFN1, GU, 0, q, ins["ffn1_w_gate"], 2 * q, 0)
            for tile, group in enumerate((list(V)[1:8], ("rg_conv_w", "m_conv_w"), ("m_norm", "m_skip"))):
                each = VROWS[tile + 1] // len(group)
                for i, name in enumerate(group):
                    sp.dma_start(vraw[each * i:each * (i + 1), tile + 1, :], rows_of(name))\
                        .then_inc(part_loaded[tile + 1], 16)
            sp.dma_start(wif_raw[:, :, :], ins["w_in"][0, :, COL["if"]:COL["if"] + 2 * HEADS]
                         .rearrange("(k p) c -> p k c", p=P)).then_inc(misc_loaded, 16)
            for c, name in enumerate(("m_b_i", "m_b_f")):
                sp.dma_start(bif[:, c:c + 1], ins[name].rearrange("a h -> h a")).then_inc(misc_loaded, 16)
            ffn_loads(S_FFN1, ins["ffn1_w_gate"], ins["ffn1_w_up"], ins["ffn1_w_down"])

            def mixer(i, first):
                n = i - first
                for j in range(MX):
                    if j == 9:
                        if isinstance(n, int):
                            sp.wait_ge(slot_used, S_MIX)
                        else:
                            sp.wait_ge(mm["C"], C_MIX - 1 + 8 * n)
                        for m, name in enumerate(("m_w_q", "m_w_k", "m_w_v")):
                            sp.dma_start(w_heads[:, m, :, :],
                                         ins[name][0, ds(2 * n, 2)].rearrange("h (k p) e -> p (h k) e", p=P))\
                                .then_inc(qkv_loaded, 16)
                    if j == 26:
                        sp.wait_ge(mm["C"], C_MIX + 8 * n + 3)
                        for m, name in enumerate(("rg_w_a", "rg_w_x")):
                            sp.dma_start(w_heads[:, m, :, :],
                                         ins[name][0, ds(2 * n, 2)].rearrange("h (k p) e -> p (h k) e", p=P))\
                                .then_inc(ax_loaded, 16)
                    part = ("m_x", "rg_x", "m_o", "rg_gate")[j // 8]
                    load(S_MIX, MX, i, j, ins["w_in"], 2 * (j % 8), COL[part], first)
            mixer(0, 0)
            with sp.Fori(2, DB + 1) as i:
                mixer(i, 1)
            for base, gate, w in ((S_PRG, "gate_rg", "w_proj_rg"), (S_PM, "gate_m", "w_proj_m")):
                with sp.Fori(1, DB + 1) as i:
                    for j in range(PJ):
                        if j < 8:
                            load(base, PJ, i, j, ins["w_in"], 2 * j, COL[gate], 1)
                        else:
                            load(base, PJ, i, j, ins[w], 2 * (j - 8), 0, 1)
            for q in range(DB):
                for j in range(8):
                    load(S_WO, 8, q, j, ins["w_out"], 2 * j, 0)
            ffn_loads(S_FFN2, ins["ffn2_w_gate"], ins["ffn2_w_up"], ins["ffn2_w_down"], last=True)
            o = out[0].rearrange("(t p) d -> p t d", p=P)
            for k in range(2 * HALVES):
                sp.wait_ge(out_ready, k + 1)
                c = (k // 2) * DM // 2
                sp.dma_start(o[:, k % 2, c:c + DM // 2], h[:, k % 2, c:c + DM // 2]).then_inc(out_done, 16)
            sp.wait_ge(out_done, 16 * HALVES * 2)

        @block.gpsimd
        def _(pool):
            st = Steps(pool, pool_step)
            st.then(nc.gpsimd.memset(ident[:, :], 0.0))
            nc.gpsimd.affine_select(out=ident[:, :], in_=ident[:, :], compare_op=ALU.not_equal, fill=1.0,
                                    base=0, pattern=[[-1, P]], channel_multiplier=1).then_inc(consts_ready, 1)
            nc.gpsimd.memset(eps[:, :], EPS).then_inc(consts_ready, 1)
            nc.gpsimd.memset(xT[:, :, 0:PAD], 0.0).then_inc(consts_ready, 1)
            st.then(nc.gpsimd.memset(sel[:, :, :], 0.0))
            nc.gpsimd.affine_select(out=sel[:, :, :], in_=sel[:, :, :], compare_op=ALU.not_equal, fill=1.0,
                                    base=0, pattern=[[-1, HEADS], [0, P]], channel_multiplier=1)\
                .then_inc(sel_ready, 1)
            pool.wait_ge(ev["D"], D_PREP + N_PREP)
            for lo in (0, SEQ):
                nc.gpsimd.affine_select(out=decay[:, :, lo:lo + P], in_=decay[:, :, lo:lo + P],
                                        compare_op=ALU.is_ge, fill=0.0, base=0,
                                        pattern=[[0, HEADS], [1, P]], channel_multiplier=-1)\
                    .then_inc(prep["masked"], 1)

        @block.scalar
        def _(act):
            A = nc.scalar.activation
            st = Steps(act, act_step)

            def hi(base, per, i, j):
                s, r, turn = slot(base, per, i, j)
                act.wait_ge(w_loaded[r], turn * 16)
                wait(act, slot_used, s - RING + 1)
                A(w_hi[:, r, :, :], w_raw[:, r, :, :], ACT.Copy).then_inc(hi_ready, 1)

            def run(base, per, i, hooks):
                for j in range(per):
                    hi(base, per, i, j)
                    for f in hooks.get(j, ()):
                        f()

            def split_plain(pair, use, dst, col):
                act.wait_ge(mm[pair], use + 1)
                for k in range(2):
                    A(dst[:, ds(col + 2 * k, 2), :],
                      ps[PAIR[pair][k]][:, :].rearrange("p (a t) -> p a t", a=2), ACT.Copy)\
                        .then_inc(split_hi, 1)

            def norm_block(m, q, pair, use):
                if m:
                    act.wait_ge(ev["AB"[q % 2]], RES[m] + q // 2 + 1)
                if m < 3:
                    act.wait_ge(mm[pair], use + 1)
                    for k in range(TPB):
                        kt = TPB * q + k
                        ins_ = A(uT_hi[:, kt, :], ps[PAIR[pair][k // 2]][:, (k % 2) * SEQ:(k % 2 + 1) * SEQ],
                                 ACT.Copy, scale=vec[:, m, kt:kt + 1])
                        if k % 2:
                            ins_.then_inc(split_hi, 1)
                for t in range(HALVES):
                    wait(act, sq_ready, HALVES * (DB * m + q) + t)
                    A(junk[:, :], h[:, t, q * NB:(q + 1) * NB], ACT.Square, accum_out=ssq[:, m, t, q:q + 1])\
                        .then_inc(sq_ready, 1)

            def norm_root(m):
                act.wait_ge(ssum_ready, m + 1)
                A(ms[:, m, :], ms[:, m, :], ACT.Sqrt, bias=eps[:, 0:1], scale=1.0 / DM).then_inc(root_ready, 1)

            def params():
                act.wait_ge(lam_ready, 1)
                st.then(A(spl[:, 1, :], spl[:, 0, :], ACT.Exp))
                A(spl[:, 1, :], spl[:, 1, :], ACT.Ln, bias=1.0).then_inc(lam_act, 1)
                act.wait_ge(misc_loaded, 48)
                A(wif_hi[:, :, :], wif_raw[:, :, :], ACT.Copy).then_inc(wif_hi_ready, 1)

            def x_block(q):
                act.wait_ge(x_loaded[q], 16)
                norm_block(0, q, *X_USE[q])

            act.dma_start(vraw[0:KT, 0, :], ins["ffn1_norm"].rearrange("a (k p) -> (a k) p", p=P))\
                .then_inc(part_loaded[0], 16)
            act.wait_ge(consts_ready, 3)
            act.wait_ge(ev["C"], 1)
            x_block(0)

            def ffn(f, tail):
                base, a0, c0, m = ((S_FFN1, AB["ffn1"], C_FFN1, 0), (S_FFN2, AB["ffn2"], C_FFN2, 2))[f]

                def hid_hi_of(i):
                    return lambda: split_plain("C", c0 + i, hid_hi, TPB * i)

                def body(i, tail_):
                    def silu():
                        act.wait_ge(slot_used, base + 8 + GU * i)
                        wait(act, ev["B"], a0 + i)
                        act.wait_ge(rstd_ready, m + 1)
                        for t in range(HALVES):
                            ins_ = A(sg[:, t, :], ps[PAIR["A"][t]][:, :], ACT.Silu, scale=rstd[:, m, t:t + 1])
                        ins_.then_inc(ev["A"], 1)
                    hooks = {11: [silu], **tail_}
                    run(base, GU, i, hooks)
                body(0, tail)
                with act.Fori(1, FB) as i:
                    body(i, {7: [hid_hi_of(i - 1)]})
                project(base + GU * FB, DN, 2 * f + 1, {7: [hid_hi_of(FB - 1)]}, C_DN1)

            def project(base, per, m, tail, c0):
                for q in range(DB):
                    hooks = dict(tail) if q == 0 else {7: [lambda q=q: norm_block(m, q - 1, "C", c0 + q - 1)]}
                    run(base, per, q, hooks)

            def norm_tail(m, c0):
                return {7: [lambda: norm_block(m, DB - 1, "C", c0 + DB - 1)], 9: [lambda: norm_root(m)]}

            ffn(0, {1: [lambda: x_block(1)], 3: [lambda: x_block(2)], 5: [lambda: x_block(3)],
                    7: [lambda: norm_root(0)], 8: [params]})

            def gate_prep_hooks():
                def e1():
                    act.wait_ge(prep["rows"], 1)
                    st.then(A(hr[:, 2, :], hr[:, 1, :], ACT.Exp))
                    A(hr[:, 2, :], hr[:, 2, :], ACT.Ln, bias=1.0).then_inc(prep["ln"], 1)

                def e2():
                    act.wait_ge(prep["cols"], 1)
                    A(hs[:, 2, :], hs[:, 2, :], ACT.Exp).then_inc(prep["exp"], 1)

                def e3(g):
                    act.wait_ge(ev["D"], D_PREP + 3)
                    act.wait_ge(mm["D"], D_PREP + 3 + g + 1)
                    for hh in range(4):
                        head = 4 * g + hh
                        bank = ps[PAIR["D"][hh // 2]]
                        c = (hh % 2) * SEQ
                        A(decay[:, head, 0:SEQ], bank[:, c:c + SEQ], ACT.Exp, bias=colc[:, 0, head:head + 1])
                        ins_ = A(decay[:, head, SEQ:ECOL], bank[:, c + P:c + SEQ], ACT.Exp,
                                 bias=colc[:, 1, head:head + 1])
                    ins_.then_inc(ev["D"], 1)
                return {14: [e1, e2], 17: [lambda: e3(0)], 19: [lambda: e3(1)]}

            def rg_tail(n):
                def ri():
                    act.wait_ge(mm["D"], D_MIX + 5 * n + 5)
                    for k in range(TPB):
                        ins_ = A(b3[:, k, :], ps[PAIR["D"][k // 2]][:, (k % 2) * SEQ:(k % 2 + 1) * SEQ],
                                 ACT.Sigmoid, bias=cur[:, V["rg_b_a"], k:k + 1])
                    ins_.then_inc(ev["D"], 1)
                    act.wait_ge(mm["C"], C_MIX + 8 * n + 7)
                    for k in range(TPB):
                        ins_ = A(b6[:, k, :], ps[PAIR["C"][k // 2]][:, (k % 2) * SEQ:(k % 2 + 1) * SEQ],
                                 ACT.Sigmoid, bias=cur[:, V["rg_b_x"], k:k + 1])
                    ins_.then_inc(ev["C"], 1)

                def at():
                    act.wait_ge(ev["D"], D_MIX + 5 * n + 5)
                    for k in range(TPB):
                        ins_ = A(b4[:, k, :], b3[:, k, :], ACT.Exp, scale=cur[:, V["rg_lambda"], k:k + 1])
                    ins_.then_inc(mx["at"], 1)
                    for k in range(TPB):
                        ins_ = A(b3[:, k, :], b3[:, k, :], ACT.Tanh, scale=cur[:, V["rg_lambda"], k:k + 1])
                    ins_.then_inc(mx["at"], 1)

                def root():
                    act.wait_ge(mx["neg"], n + 1)
                    A(b5[:, :, :], b5[:, :, :], ACT.Sqrt, scale=-1.0).then_inc(mx["beta_root"], 1)

                def gelu():
                    act.wait_ge(slot_used, S_MIX + 32 + MX * n)
                    act.wait_ge(mm["C"], C_MIX + 8 * n + 6)
                    for t in range(HALVES):
                        ins_ = A(tok[:, t, :], ps[PAIR["B"][t]][:, :], ACT.Gelu_apprx_tanh,
                                 scale=rstd[:, 1, t:t + 1])
                    ins_.then_inc(ev["B"], 1)

                def yr():
                    act.wait_ge(ev["C"], C_MIX + 8 + 8 * n)
                    A(yr_hi[:, ds(TPB * n, TPB), :], b6[:, :, :], ACT.Copy).then_inc(mx["yr_hi"], 1)
                return {0: [ri], 2: [at], 4: [gelu], 5: [root], 9: [yr]}

            def mixer(n, tail):
                c, d, ab = C_MIX + 8 * n, D_MIX + 5 * n, AB["mix"] + 2 * n

                def m_x():
                    act.wait_ge(slot_used, S_MIX + 8 + MX * n)
                    act.wait_ge(rstd_ready, 2)
                    wait(act, mm["C"], c)
                    for t in range(HALVES):
                        ins_ = A(tok[:, t, :], ps[PAIR["A"][t]][:, :], ACT.Copy, scale=rstd[:, 1, t:t + 1])
                    ins_.then_inc(ev["A"], 1)

                def to_xT(pair, use):
                    act.wait_ge(mm[pair], use + 1)
                    for k in range(2):
                        ins_ = A(xT[:, 2 * k:2 * k + 2, PAD:PAD + SEQ],
                                 ps[PAIR[pair][k]][:, :].rearrange("p (a t) -> p a t", a=2), ACT.Copy)
                    ins_.then_inc(ev[pair], 1)

                def v_out():
                    act.wait_ge(mm["C"], c + 2)
                    for t in range(HALVES):
                        ins_ = A(vtok[:, t, :, 0:HD], ps[PAIR["C"][t]][:, :].rearrange("p (a e) -> p a e", a=2),
                                 ACT.Copy)
                    ins_.then_inc(ev["C"], 1)

                def silu():
                    act.wait_ge(mx["conv_m"], n + 1)
                    A(xc[:, :, :], xc[:, :, :], ACT.Silu).then_inc(mx["silu"], 1)

                def q_out():
                    act.wait_ge(mm["D"], d + 1)
                    for k in range(2):
                        ins_ = A(b4[:, 2 * k:2 * k + 2, :],
                                 ps[PAIR["D"][k]][:, :].rearrange("p (a t) -> p a t", a=2), ACT.Copy)
                    ins_.then_inc(ev["D"], 1)

                def root():
                    act.wait_ge(mx["var"], n + 1)
                    A(small[:, 6, :], small[:, 6, :], ACT.Sqrt, bias=eps[:, 0:1]).then_inc(mx["root"], 1)

                def rg_x():
                    act.wait_ge(slot_used, S_MIX + 16 + MX * n)
                    act.wait_ge(mm["C"], c + 1)
                    for t in range(HALVES):
                        ins_ = A(tok[:, t, :], ps[PAIR["B"][t]][:, :], ACT.Copy, scale=rstd[:, 1, t:t + 1])
                    ins_.then_inc(ev["B"], 1)

                def m_o():
                    act.wait_ge(slot_used, S_MIX + 24 + MX * n)
                    act.wait_ge(mm["D"], d + 4)
                    for t in range(HALVES):
                        ins_ = A(tok[:, t, :], ps[PAIR["A"][t]][:, :], ACT.Sigmoid, scale=rstd[:, 1, t:t + 1])
                    ins_.then_inc(ev["A"], 1)

                def ym():
                    act.wait_ge(ev["C"], c + 6)
                    A(ym_hi[:, ds(TPB * n, TPB), :], b2[:, :, :], ACT.Copy).then_inc(mx["ym_hi"], 1)
                z = 2 if tail is first else 0
                own = {11: [m_x], 12: [lambda: to_xT("C", c)], 14: [v_out], 15: [silu], 18 + z: [q_out],
                       23 + z: [root], 24: [rg_x], 27 + z // 2: [lambda: to_xT("D", d + 3)],
                       28 + z // 2: [m_o], 31: [ym]}
                hooks = {}
                for part in (tail, own):
                    for j, fs in part.items():
                        hooks.setdefault(j, []).extend(fs)
                run(S_MIX, MX, n, hooks)

            first = norm_tail(1, C_DN1)
            for j, fs in gate_prep_hooks().items():
                first.setdefault(j, []).extend(fs)
            mixer(0, first)
            with act.Fori(1, DB) as n:
                mixer(n, rg_tail(n - 1))

            def gated(base, ab0, tail, c0):
                def body(n, tail_):
                    def sig():
                        act.wait_ge(slot_used, base + 8 + PJ * n)
                        wait(act, ev["B"], ab0 + n)
                        for t in range(HALVES):
                            ins_ = A(sg[:, t, :], ps[PAIR["A"][t]][:, :], ACT.Sigmoid, scale=rstd[:, 1, t:t + 1])
                        ins_.then_inc(ev["A"], 1)
                    run(base, PJ, n, {11: [sig], **tail_})
                body(0, tail)
                with act.Fori(1, DB) as n:
                    body(n, {} if c0 is None else {7: [lambda: split_plain("C", c0 + n - 1, mg_hi, TPB * (n - 1))]})
            gated(S_PRG, AB["prg"], rg_tail(DB - 1), None)
            gated(S_PM, AB["pm"], {}, C_PM)
            project(S_WO, 8, 2, {7: [lambda: split_plain("C", C_PM + DB - 1, mg_hi, TPB * (DB - 1))]}, C_WO)
            ffn(1, norm_tail(2, C_WO))
            norm_block(3, DB - 1, None, None)
            norm_root(3)

        @block.vector
        def _(dve):
            v = nc.vector
            st = Steps(dve, dve_step)

            def lo(base, per, i, j):
                s, r, _ = slot(base, per, i, j)
                dve.wait_ge(hi_ready, s + 1)
                wait(dve, slot_used, s - RING + 1)
                v.tensor_tensor(w_lo[:, r, :, :], w_raw[:, r, :, :], w_hi[:, r, :, :].bitcast(f32),
                                ALU.subtract).then_inc(lo_ready, 1)

            def run(base, per, i, hooks):
                for j in range(per):
                    lo(base, per, i, j)
                    for f in hooks.get(j, ()):
                        f()

            def split_plain(pair, sp0, dst_hi, dst_lo, col):
                for k in range(2):
                    dve.wait_ge(split_hi, 2 * sp0 + k + 1)
                    ins_ = v.tensor_tensor(dst_lo[:, ds(col + 2 * k, 2), :],
                                           ps[PAIR[pair][k]][:, :].rearrange("p (a t) -> p a t", a=2),
                                           dst_hi[:, ds(col + 2 * k, 2), :].bitcast(f32), ALU.subtract)
                ins_.then_inc(ev[pair], 1)

            def norm_block(m, q, pair, sp0):
                for k in range(TPB):
                    kt = TPB * q + k
                    dve.wait_ge(split_hi, 2 * sp0 + k // 2 + 1)
                    ins_ = v.scalar_tensor_tensor(
                        out=uT_lo[:, kt, :], in0=ps[PAIR[pair][k // 2]][:, (k % 2) * SEQ:(k % 2 + 1) * SEQ],
                        scalar=vec[:, m, kt:kt + 1], in1=uT_hi[:, kt, :].bitcast(f32),
                        op0=ALU.mult, op1=ALU.subtract)
                ins_.then_inc(ev[pair], 1)

            def norm_sum(m):
                dve.wait_ge(sq_ready, HALVES * DB * (m + 1))
                v.tensor_reduce(out=ms[:, m, :], in_=ssq[:, m, :, :], op=ALU.add, axis=AX).then_inc(ssum_ready, 1)

            def norm_rstd(m):
                dve.wait_ge(root_ready, m + 1)
                v.reciprocal(rstd[:, m, :], ms[:, m, :]).then_inc(rstd_ready, 1)

            def residual(m, q, scale):
                pair = "AB"[q % 2]
                dve.wait_ge(slot_used, RES_SLOT[m][0] + RES_SLOT[m][1] * (q + 1))
                for t in range(HALVES):
                    cols = slice(q * NB, (q + 1) * NB)
                    ins_ = v.scalar_tensor_tensor(out=h[:, t, cols], in0=ps[PAIR[pair][t]][:, :], scalar=scale,
                                                  in1=h[:, t, cols], op0=ALU.mult, op1=ALU.add)
                ins_.then_inc(ev[pair], 1)

            def params():
                dve.wait_ge(mm["C"], 3)
                v.tensor_copy(vec[:, 1:NV, :], ps[4][:, 0:(NV - 1) * KT].rearrange("p (v k) -> p v k", k=KT))\
                    .then_inc(ev["C"], 1)
                dve.wait_ge(ev["C"], 3)
                lam = vec[:, V["rg_lambda"], :]
                v.tensor_scalar(spl[:, 2, :], lam, -1.0, 0.0, ALU.mult, ALU.max)
                v.scalar_tensor_tensor(out=spl[:, 0, :], in0=lam, scalar=-1.0, in1=lam, op0=ALU.mult, op1=ALU.min)\
                    .then_inc(lam_ready, 1)

            def params2():
                lam = vec[:, V["rg_lambda"], :]
                dve.wait_ge(lam_act, 1)
                st.then(v.tensor_tensor(spl[:, 2, :], spl[:, 2, :], spl[:, 1, :], ALU.add))
                st.then(v.tensor_scalar(lam, spl[:, 2, :], -RG_C, None, ALU.mult))
                dve.wait_ge(wif_hi_ready, 1)
                v.tensor_tensor(wif_lo[:, :, :], wif_raw[:, :, :], wif_hi[:, :, :].bitcast(f32), ALU.subtract)\
                    .then_inc(wif_ready, 1)

            def x_block(q):
                norm_block(0, q, X_USE[q][0], SP["x"] + q)

            dve.wait_ge(mm["C"], 1)
            v.tensor_copy(vec[:, 0, :], ps[4][:, 0:KT]).then_inc(ev["C"], 1)
            x_block(0)

            def project(base, per, m, tail, c, scale):
                for q in range(DB):
                    hooks = {} if q else dict(tail)
                    if q:
                        hooks[3] = [lambda q=q: residual(m, q - 1, scale)]
                        if m != 3:
                            hooks[7] = [lambda q=q: norm_block(m, q - 1, "C", SP[c] + q - 1)]
                    run(base, per, q, hooks)

            def norm_tail(m, c, scale):
                return {3: [lambda: residual(m, DB - 1, scale)],
                        7: [lambda: norm_block(m, DB - 1, "C", SP[c] + DB - 1)],
                        8: [lambda: norm_sum(m)], 9: [lambda: norm_rstd(m)]}

            def ffn(f, tail):
                base, a0, c0, m, sp0 = ((S_FFN1, AB["ffn1"], C_FFN1, 0, SP["ffn1"]),
                                        (S_FFN2, AB["ffn2"], C_FFN2, 2, SP["ffn2"]))[f]

                def hidden(i):
                    dve.wait_ge(slot_used, base + GU + GU * i)
                    dve.wait_ge(ev["A"], a0 + 1 + i)
                    dve.wait_ge(mm["C"], c0 + i)
                    for t in range(HALVES):
                        ins_ = v.scalar_tensor_tensor(out=tok[:, t, :], in0=ps[PAIR["B"][t]][:, :],
                                                      scalar=rstd[:, m, t:t + 1], in1=sg[:, t, :],
                                                      op0=ALU.mult, op1=ALU.mult)
                    ins_.then_inc(ev["B"], 1)

                def after(i):
                    return {3: [lambda: hidden(i)],
                            7: [lambda: split_plain("C", sp0 + i, hid_hi, hid_lo, TPB * i)]}
                run(base, GU, 0, tail)
                with dve.Fori(1, FB) as i:
                    run(base, GU, i, after(i - 1))
                project(base + GU * FB, DN, 2 * f + 1, after(FB - 1), "dn1", 0.5)

            ffn(0, {1: [lambda: x_block(1)], 3: [lambda: x_block(2)], 5: [params, lambda: x_block(3)],
                    7: [lambda: norm_sum(0)], 8: [lambda: norm_rstd(0)], 9: [params2]})

            def prep_hooks():
                def gates():
                    dve.wait_ge(mm["D"], D_PREP + 1)
                    for t in range(HALVES):
                        ins_ = v.tensor_scalar(gtok[:, t, :], ps[6][:, t * 2 * HEADS:(t + 1) * 2 * HEADS],
                                               rstd[:, 1, t:t + 1], None, ALU.mult)
                    ins_.then_inc(ev["D"], 1)

                def rows():
                    dve.wait_ge(mm["D"], D_PREP + 2)
                    v.tensor_scalar(hr[:, 0, :], ps[6][0:HEADS, 0:SEQ], bif[:, 0:1], None, ALU.add)
                    v.tensor_scalar(hr[:, 3, :], ps[7][0:HEADS, 0:SEQ], bif[:, 1:2], None, ALU.add)\
                        .then_inc(ev["D"], 1)
                    dve.wait_ge(ev["D"], D_PREP + 2)
                    v.scalar_tensor_tensor(out=hr[:, 1, :], in0=hr[:, 3, :], scalar=-1.0, in1=hr[:, 3, :],
                                           op0=ALU.mult, op1=ALU.min).then_inc(prep["rows"], 1)
                    st.then(v.memset(hs[:, 0, :], 1.0))
                    dve.wait_ge(prep["ln"], 1)
                    st.then(v.scalar_tensor_tensor(out=hr[:, 1, :], in0=hr[:, 3, :], scalar=0.0, in1=hr[:, 2, :],
                                                   op0=ALU.min, op1=ALU.subtract))
                    st.then(v.tensor_tensor_scan(hs[:, 1, :], hs[:, 0, :], hr[:, 1, :], 0.0, ALU.mult, ALU.add))
                    st.then(v.tensor_tensor(hr[:, 0, :], hr[:, 0, :], hs[:, 1, :], ALU.subtract))
                    st.then(v.tensor_tensor_scan(hr[:, 2, :], hr[:, 0, :], hr[:, 0, :], 0.0, ALU.max, ALU.max))
                    v.tensor_scalar(hr[:, 3, :], hr[:, 2, :], -1.0, None, ALU.mult)
                    v.scalar_tensor_tensor(out=hs[:, 2, :], in0=hs[:, 1, :], scalar=-1.0, in1=hr[:, 2, :],
                                           op0=ALU.mult, op1=ALU.subtract).then_inc(prep["cols"], 1)

                def cols():
                    dve.wait_ge(mm["D"], D_PREP + 3)
                    v.tensor_copy(colc[:, :, :], ps[6][:, 0:HALVES * HEADS].rearrange("p (t h) -> p t h", h=HEADS))
                    v.tensor_copy(cole[:, :, :], ps[7][:, 0:HALVES * HEADS].rearrange("p (t h) -> p t h", h=HEADS))\
                        .then_inc(ev["D"], 1)
                return {12: [gates], 13: [rows], 15: [cols]}

            def rg_tail(n):
                def neg():
                    dve.wait_ge(mx["at"], 2 * n + 1)
                    st.then(v.tensor_tensor(b5[:, :, :], b4[:, :, :], b4[:, :, :], ALU.mult))
                    dve.wait_ge(mx["at"], 2 * n + 2)
                    v.scalar_tensor_tensor(out=b5[:, :, :], in0=b5[:, :, :], scalar=1.0, in1=b3[:, :, :],
                                           op0=ALU.add, op1=ALU.mult).then_inc(mx["neg"], 1)
                    dve.wait_ge(ev["C"], C_MIX + 8 * n + 7)
                    st.then(v.tensor_tensor(b6[:, :, :], b6[:, :, :], xc[:, :, :], ALU.mult))

                def scan():
                    dve.wait_ge(mx["beta_root"], n + 1)
                    st.then(v.tensor_tensor(b6[:, :, :], b5[:, :, :], b6[:, :, :], ALU.mult))
                    for k in range(TPB):
                        ins_ = v.tensor_tensor_scan(b2[:, k, :], b4[:, k, :], b6[:, k, :], 0.0, ALU.mult, ALU.add)
                    st.then(ins_)

                def yr():
                    dve.wait_ge(mm["C"], C_MIX + 8 * n + 8)
                    for k in range(2):
                        ins_ = v.tensor_tensor(b6[:, 2 * k:2 * k + 2, :],
                                               ps[PAIR["C"][k]][:, :].rearrange("p (a t) -> p a t", a=2),
                                               b2[:, 2 * k:2 * k + 2, :], ALU.mult)
                    ins_.then_inc(ev["C"], 1)

                def yr_lo_():
                    dve.wait_ge(mx["yr_hi"], n + 1)
                    v.tensor_tensor(yr_lo[:, ds(TPB * n, TPB), :], b6[:, :, :],
                                    yr_hi[:, ds(TPB * n, TPB), :].bitcast(f32), ALU.subtract).then_inc(mx["yr_lo"], 1)
                return {3: [neg], 6: [scan], 8: [yr], 10: [yr_lo_]}

            def mixer(n, tail):
                c, d = C_MIX + 8 * n, D_MIX + 5 * n

                def current():
                    wait(dve, mx["at"], 2 * n)
                    st.then(v.tensor_copy(cur[:, :, :], vec[:, :, ds(TPB * n, TPB)]))

                def conv(wname, bname, done):
                    w, b = V[wname], V[bname]
                    for k in range(TPB):
                        ins_ = v.tensor_scalar(xc[:, k, :], xT[:, k, 0:SEQ], cur[:, w, k:k + 1], cur[:, b, k:k + 1],
                                               ALU.mult, ALU.add)
                    st.then(ins_)
                    for g in range(1, CW):
                        for k in range(TPB):
                            ins_ = v.scalar_tensor_tensor(out=xc[:, k, :], in0=xT[:, k, g:g + SEQ],
                                                          scalar=cur[:, w + g, k:k + 1], in1=xc[:, k, :],
                                                          op0=ALU.mult, op1=ALU.add)
                        if g < CW - 1:
                            st.then(ins_)
                    ins_.then_inc(done, 1)

                def conv_m():
                    v.memset(vtok[:, :, :, HD:HD + 2], 1.0)
                    dve.wait_ge(ev["C"], c + 1)
                    conv("m_conv_w", "m_conv_b", mx["conv_m"])

                def skip():
                    dve.wait_ge(mx["silu"], n + 1)
                    dve.wait_ge(mm["D"], d)
                    for k in range(TPB):
                        ins_ = v.tensor_scalar(b2[:, k, :], xc[:, k, :], cur[:, V["m_skip"], k:k + 1], None, ALU.mult)
                    st.then(ins_)

                def k_out():
                    dve.wait_ge(mm["C"], c + 3)
                    for k in range(2):
                        ins_ = v.tensor_scalar(b5[:, 2 * k:2 * k + 2, :],
                                               ps[PAIR["C"][k]][:, :].rearrange("p (a t) -> p a t", a=2),
                                               float(HD) ** -0.5, None, ALU.mult)
                    ins_.then_inc(ev["C"], 1)

                def scores():
                    dve.wait_ge(prep["masked"], 2)
                    dve.wait_ge(mm["D"], d + 2)
                    for hh in range(2):
                        ins_ = v.tensor_tensor(sdec[:, hh, :], ps[PAIR["D"][hh]][:, 0:ECOL],
                                               decay[:, ds(2 * n + hh, 1), :].rearrange("p a c -> p (a c)"), ALU.mult)
                    ins_.then_inc(ev["D"], 1)

                def stats():
                    dve.wait_ge(mm["D"], d + 3)
                    st.then(v.tensor_copy(small[:, 4, :].rearrange("p (h t) -> p h t", h=2),
                                          cole[:, :, ds(2 * n, 2)].rearrange("p t h -> p h t")))
                    for hh in range(2):
                        for t in range(HALVES):
                            b, g = ps[PAIR["CD"[hh]][t]], 2 * hh + t
                            v.tensor_tensor(small[:, 5, g:g + 1], b[:, HD:HD + 1], small[:, 4, g:g + 1], ALU.max)
                            ins_ = v.bn_stats(bn[:, g, :], b[:, 0:HD])
                    st.then(ins_)
                    for hh in range(2):
                        for t in range(HALVES):
                            b, g = ps[PAIR["CD"[hh]][t]], 2 * hh + t
                            v.scalar_tensor_tensor(out=small[:, 5, g:g + 1], in0=b[:, HD:HD + 1], scalar=-1.0,
                                                   in1=small[:, 5, g:g + 1], op0=ALU.mult, op1=ALU.max)
                            ins_ = v.bn_aggr(mv[:, g, :], bn[:, g, :])
                    st.then(ins_)
                    st.then(v.reciprocal(small[:, 5, :], small[:, 5, :]))
                    st.then(v.tensor_tensor(small[:, 6, :], small[:, 5, :], small[:, 5, :], ALU.mult))
                    v.tensor_tensor(small[:, 6, :], small[:, 6, :], mv[:, :, 1], ALU.mult).then_inc(mx["var"], 1)

                def apply():
                    dve.wait_ge(mx["root"], n + 1)
                    st.then(v.reciprocal(small[:, 7, :], small[:, 6, :]))
                    st.then(v.tensor_tensor(small[:, 7, :], small[:, 7, :], small[:, 5, :], ALU.mult))
                    for hh in range(2):
                        for t in range(HALVES):
                            b, g = ps[PAIR["CD"[hh]][t]], 2 * hh + t
                            ins_ = v.tensor_scalar(b4tok[:, t, hh * HD:(hh + 1) * HD], b[:, 0:HD], mv[:, g, 0:1],
                                                   small[:, 7, g:g + 1], ALU.subtract, ALU.mult)
                        ins_.then_inc(ev["CD"[hh]], 1)

                def s_out():
                    dve.wait_ge(mm["C"], c + 5)
                    for k in range(TPB):
                        ins_ = v.scalar_tensor_tensor(
                            out=b5[:, k, :], in0=ps[PAIR["C"][k // 2]][:, (k % 2) * SEQ:(k % 2 + 1) * SEQ],
                            scalar=cur[:, V["m_norm"], k:k + 1], in1=b2[:, k, :], op0=ALU.mult, op1=ALU.add)
                    ins_.then_inc(ev["C"], 1)

                def conv_r():
                    dve.wait_ge(ev["D"], d + 4)
                    conv("rg_conv_w", "rg_conv_b", mx["conv_r"])

                def ym():
                    dve.wait_ge(mm["C"], c + 6)
                    dve.wait_ge(ev["C"], c + 5)
                    for k in range(2):
                        ins_ = v.tensor_tensor(b2[:, 2 * k:2 * k + 2, :],
                                               ps[PAIR["C"][k]][:, :].rearrange("p (a t) -> p a t", a=2),
                                               b5[:, 2 * k:2 * k + 2, :], ALU.mult)
                    ins_.then_inc(ev["C"], 1)

                def ym_lo_():
                    dve.wait_ge(mx["ym_hi"], n + 1)
                    v.tensor_tensor(ym_lo[:, ds(TPB * n, TPB), :], b2[:, :, :],
                                    ym_hi[:, ds(TPB * n, TPB), :].bitcast(f32), ALU.subtract).then_inc(mx["ym_lo"], 1)
                z = 2 if tail is first else 0
                own = {11: [current], 13: [conv_m], 17: [skip], 18 + z: [k_out], 20 + z: [scores],
                       23 + z: [stats], 24 + z: [apply], 27 + z // 2: [s_out], 28 + z // 2: [conv_r],
                       30: [] if z else [ym], 31: [ym, ym_lo_] if z else [ym_lo_]}
                hooks = {}
                for part in (tail, own):
                    for j, fs in part.items():
                        hooks.setdefault(j, []).extend(fs)
                run(S_MIX, MX, n, hooks)

            first = norm_tail(1, "dn1", 0.5)
            for j, fs in prep_hooks().items():
                first.setdefault(j, []).extend(fs)
            mixer(0, first)
            with dve.Fori(1, DB) as n:
                st.loop(n, 1, 19)
                mixer(n, rg_tail(n - 1))
            st.leave(DB - 1)

            def gated(base, tail, after, steps):
                run(base, PJ, 0, tail)
                with dve.Fori(1, DB) as n:
                    st.loop(n, 1, steps)
                    run(base, PJ, n, after(n - 1))
                st.leave(DB - 1)

            def rg_merge(n):
                def f():
                    dve.wait_ge(slot_used, S_PRG + PJ + PJ * n)
                    dve.wait_ge(ev["A"], AB["prg"] + 1 + n)
                    for t in range(HALVES):
                        ins_ = v.tensor_tensor(merged[:, t, ds(n * NB, NB)], ps[PAIR["B"][t]][:, :], sg[:, t, :],
                                               ALU.mult)
                    ins_.then_inc(ev["B"], 1)
                return {3: [f]}

            def m_merge(n):
                def f():
                    dve.wait_ge(slot_used, S_PM + PJ + PJ * n)
                    dve.wait_ge(ev["A"], AB["pm"] + 1 + n)
                    dve.wait_ge(mm["C"], C_PM + n)
                    for t in range(HALVES):
                        ins_ = v.tensor_tensor(tok[:, t, :], ps[PAIR["B"][t]][:, :], sg[:, t, :], ALU.mult)
                    st.then(ins_)
                    for t in range(HALVES):
                        ins_ = v.tensor_tensor(tok[:, t, :], tok[:, t, :], merged[:, t, ds(n * NB, NB)], ALU.add)
                    ins_.then_inc(ev["B"], 1)
                return {3: [f], 7: [lambda: split_plain("C", SP["pm"] + n, mg_hi, mg_lo, TPB * n)]}
            gated(S_PRG, rg_tail(DB - 1), rg_merge, 0)
            gated(S_PM, rg_merge(DB - 1), m_merge, 1)
            project(S_WO, 8, 2, m_merge(DB - 1), "wo", 1.0)
            ffn(1, norm_tail(2, "wo", 1.0))
            residual(3, DB - 1, 0.5)
            norm_sum(3)
            norm_rstd(3)
            dve.wait_ge(gfin_loaded, 16)
            dve.wait_ge(rstd_ready, 4)
            for k in range(2 * HALVES):
                c = slice((k // 2) * DM // 2, (k // 2 + 1) * DM // 2)
                v.scalar_tensor_tensor(out=h[:, k % 2, c], in0=h[:, k % 2, c], scalar=rstd[:, 3, k % 2:k % 2 + 1],
                                       in1=gfin[:, c], op0=ALU.mult, op1=ALU.mult).then_inc(out_ready, 1)

        @block.tensor
        def _(pe):
            mmul = nc.tensor.matmul

            def fill(pair, use):
                wait(pe, ev[pair], use)

            def product(pair, use, base, per, i, j0, n, lhs_hi, lhs_lo, before=None, hooks=None):
                for jj in range(n):
                    j = j0 + jj
                    s, r, _ = slot(base, per, i, j)
                    for f in (before or {}).get(j, ()):
                        f()
                    if jj == 0:
                        fill(pair, use)
                    pe.wait_ge(lo_ready, s + 1)
                    for k in range(2):
                        kt = 2 * jj + k
                        for t in range(HALVES):
                            col = slice(t * P, (t + 1) * P)
                            for x, (a, w) in enumerate(((lhs_hi, w_hi), (lhs_hi, w_lo), (lhs_lo, w_hi))):
                                ins_ = mmul(ps[PAIR[pair][t]][:, :], a[:, kt, col], w[:, r, k, :],
                                            start=kt == 0 and x == 0, stop=kt == 2 * n - 1 and x == 2)
                    ins_.then_inc(slot_used, 1)
                    for f in (hooks or {}).get(j, ()):
                        f()

            def transpose(pair, src):
                for k in range(TPB):
                    for t in range(HALVES):
                        c = (k % 2) * SEQ + t * P
                        ins_ = nc.tensor.transpose(ps[PAIR[pair][k // 2]][:, c:c + P], src(t, k), ident[:, :])
                ins_.then_inc(mm[pair], 1)

            def tok_block(t, k):
                return tok[:, t, k * P:(k + 1) * P]

            def h_block(q):
                return lambda t, k: h[:, t, (TPB * q + k) * P:(TPB * q + k + 1) * P]

            def params(tiles):
                at_ = 0
                for tile in tiles:
                    rows = VROWS[tile]
                    pe.wait_ge(part_loaded[tile], 16 * (1, 7, 2, 2)[tile])
                    ins_ = nc.tensor.transpose(ps[4][:, at_:at_ + rows], vraw[0:rows, tile, :],
                                               ident[0:rows, 0:rows])
                    at_ += rows
                ins_.then_inc(mm["C"], 1)

            def x_T(q):
                pe.wait_ge(x_loaded[q], 16)
                fill(*X_USE[q])
                transpose(X_USE[q][0], h_block(q))

            def other_params():
                fill("C", 2)
                params((1, 2, 3))

            pe.wait_ge(consts_ready, 1)
            params((0,))
            x_T(0)

            def norm_T(m, q, use):
                def f():
                    pe.wait_ge(ev["AB"[q % 2]], RES[m] + q // 2 + 1)
                    fill("C", use)
                    transpose("C", h_block(q))
                return f

            def wait_u(m):
                if m == 0:
                    return {2 * q: [lambda q=q: pe.wait_ge(ev[X_USE[q][0]], X_USE[q][1] + 1)] for q in range(DB)}
                done = {1: C_DN1 + DB, 2: C_WO + DB}[m]
                return {0: [lambda: pe.wait_ge(ev["C"], done - 1)], 6: [lambda: pe.wait_ge(ev["C"], done)]}

            def project(base, per, m, a0, c0, n, lhs_hi, lhs_lo, before, hooks):
                for q in range(DB):
                    product("AB"[q % 2], a0 + q // 2, base, per, q, 0, n, lhs_hi, lhs_lo,
                            before if q == 0 else None,
                            hooks if q == 0 else ({2: [norm_T(m, q - 1, c0 + q - 1)]} if m != 3 else None))

            def ffn(f, tail):
                base, a0, c0, m = ((S_FFN1, AB["ffn1"], C_FFN1, 0), (S_FFN2, AB["ffn2"], C_FFN2, 2))[f]

                def hid_T(i):
                    def f_():
                        pe.wait_ge(ev["B"], a0 + 1 + i)
                        fill("C", c0 + i)
                        transpose("C", tok_block)
                    return f_

                def body(i, before, hooks):
                    product("A", a0 + i, base, GU, i, 0, 8, uT_hi, uT_lo, before, hooks)
                    product("B", a0 + i, base, GU, i, 8, 8, uT_hi, uT_lo, before, hooks)
                body(0, wait_u(m), tail)
                with pe.Fori(1, FB) as i:
                    body(i, None, {2: [hid_T(i - 1)]})
                project(base + GU * FB, DN, 2 * f + 1, a0 + FB, C_DN1, DN, hid_hi, hid_lo,
                        {0: [lambda: pe.wait_ge(ev["C"], c0 + FB - 1)],
                         2 * (FB - 1): [lambda: pe.wait_ge(ev["C"], c0 + FB)]},
                        {2: [hid_T(FB - 1)]})

            ffn(0, {0: [lambda: x_T(1)], 2: [lambda: x_T(2)], 3: [other_params], 4: [lambda: x_T(3)]})

            def prep_hooks():
                def gates():
                    pe.wait_ge(wif_ready, 1)
                    fill("D", D_PREP)
                    for t in range(HALVES):
                        col = slice(t * P, (t + 1) * P)
                        for kt in range(KT):
                            for x, (a, w) in enumerate(((uT_hi, wif_hi), (uT_hi, wif_lo), (uT_lo, wif_hi))):
                                ins_ = mmul(ps[6][:, t * 2 * HEADS:(t + 1) * 2 * HEADS], a[:, kt, col], w[:, kt, :],
                                            start=kt == 0 and x == 0, stop=kt == KT - 1 and x == 2)
                    ins_.then_inc(mm["D"], 1)

                def rows():
                    fill("D", D_PREP + 1)
                    for g in range(2):
                        for t in range(HALVES):
                            ins_ = nc.tensor.transpose(ps[6 + g][0:HEADS, t * P:(t + 1) * P],
                                                       gtok[:, t, g * HEADS:(g + 1) * HEADS], ident[:, :])
                    ins_.then_inc(mm["D"], 1)

                def cols():
                    fill("D", D_PREP + 2)
                    pe.wait_ge(prep["exp"], 1)
                    for g, src in enumerate((hr[:, 0, :], hs[:, 2, :])):
                        for t in range(HALVES):
                            ins_ = nc.tensor.transpose(ps[6 + g][:, t * HEADS:(t + 1) * HEADS],
                                                       src[:, t * P:(t + 1) * P], ident[0:HEADS, 0:HEADS])
                    ins_.then_inc(mm["D"], 1)

                def spread(g):
                    def f():
                        pe.wait_ge(sel_ready, 1)
                        fill("D", D_PREP + 3 + g)
                        for hh in range(4):
                            ins_ = mmul(ps[PAIR["D"][hh // 2]][:, (hh % 2) * SEQ:(hh % 2 + 1) * SEQ],
                                        sel[:, 4 * g + hh, :], hr[:, 3, :], start=True, stop=True)
                        ins_.then_inc(mm["D"], 1)
                    return f
                return {7: [gates], 9: [rows], 12: [cols], 13: [spread(0)], 15: [spread(1)]}

            def rg_tail(n):
                def gate_T():
                    pe.wait_ge(ev["B"], AB["mix"] + 2 * n + 2)
                    fill("C", C_MIX + 8 * n + 7)
                    transpose("C", tok_block)
                return {3: [gate_T]}

            def mixer(n, before, tail):
                c, d, ab = C_MIX + 8 * n, D_MIX + 5 * n, AB["mix"] + 2 * n

                def heads(pair, use, m, src):
                    fill(pair, use)
                    for hh in range(2):
                        for e in range(2):
                            for k in range(2):
                                ins_ = mmul(ps[PAIR[pair][hh]][:, e * SEQ:(e + 1) * SEQ],
                                            w_heads[:, m, 2 * hh + k, e * P:(e + 1) * P], src[:, 2 * hh + k, :],
                                            start=k == 0, stop=k == 1)
                    ins_.then_inc(mm[pair], 1)

                def mx_T():
                    pe.wait_ge(ev["A"], ab + 1)
                    fill("C", c)
                    transpose("C", tok_block)

                def v_mm():
                    pe.wait_ge(qkv_loaded, 48 + 48 * n)
                    fill("C", c + 1)
                    for t in range(HALVES):
                        for hh in range(2):
                            for k in range(2):
                                ins_ = mmul(ps[PAIR["C"][t]][:, hh * HD:(hh + 1) * HD],
                                            xT[:, 2 * hh + k, PAD + t * P:PAD + (t + 1) * P],
                                            w_heads[:, 2, 2 * hh + k, :], start=k == 0, stop=k == 1)
                    ins_.then_inc(mm["C"], 1)

                def qk_mm():
                    pe.wait_ge(mx["silu"], n + 1)
                    heads("D", d, 0, xc)
                    heads("C", c + 2, 1, xc)

                def s_mm():
                    pe.wait_ge(ev["C"], c + 3)
                    fill("D", d + 1)
                    for hh in range(2):
                        for s in range(2):
                            for e in range(2):
                                ins_ = mmul(ps[PAIR["D"][hh]][:, s * SEQ:s * SEQ + SEQ - s * P],
                                            b5[:, 2 * hh + e, s * P:(s + 1) * P], b4[:, 2 * hh + e, s * P:SEQ],
                                            start=e == 0, stop=e == 1)
                    ins_.then_inc(mm["D"], 1)

                def num_mm():
                    fill("C", c + 3)
                    fill("D", d + 2)
                    for hh in range(2):
                        b = PAIR["CD"[hh]]
                        mmul(ps[b[0]][:, 0:HD + 2], sdec[:, hh, 0:P], vtok[:, 0, hh, :], start=True, stop=True)
                        mmul(ps[b[1]][:, 0:HD + 2], sdec[:, hh, P:SEQ], vtok[:, 0, hh, :], start=True, stop=False)
                        mmul(ps[b[1]][:, 0:HD + 2], sdec[:, hh, SEQ:ECOL], vtok[:, 1, hh, :], start=False, stop=True)\
                            .then_inc(mm["CD"[hh]], 1)

                def s_T():
                    pe.wait_ge(ev["D"], d + 3)
                    fill("C", c + 4)
                    transpose("C", lambda t, k: b4tok[:, t, k * P:(k + 1) * P])

                def rgx_T():
                    pe.wait_ge(ev["B"], ab + 1)
                    fill("D", d + 3)
                    transpose("D", tok_block)

                def mo_T():
                    pe.wait_ge(ev["A"], ab + 2)
                    fill("C", c + 5)
                    transpose("C", tok_block)

                def wa_mm():
                    pe.wait_ge(ax_loaded, 32 + 32 * n)
                    pe.wait_ge(mx["conv_r"], n + 1)
                    heads("D", d + 4, 0, xc)

                def wx_mm():
                    heads("C", c + 6, 1, xc)
                z = 2 if tail is first else 0
                own = {8: [mx_T], 10: [v_mm], 14 + z: [qk_mm], 16 + z: [s_mm], 19 + z: [num_mm],
                       23 + z // 2: [s_T, rgx_T], 26 + z // 2: [mo_T], 28 + z // 2: [wa_mm], 29 + z // 2: [wx_mm]}
                hooks = {}
                for part in (tail, own):
                    for j, fs in part.items():
                        hooks.setdefault(j, []).extend(fs)
                assert max(hooks) < MX
                for b, pair in enumerate("ABAB"):
                    product(pair, ab + b // 2, S_MIX, MX, n, 8 * b, 8, uT_hi, uT_lo, before, hooks)

            first = {2: [norm_T(1, DB - 1, C_DN1 + DB - 1)], **prep_hooks()}
            mixer(0, wait_u(1), first)
            with pe.Fori(1, DB) as n:
                mixer(n, None, rg_tail(n - 1))

            def gated(base, ab0, lhs_hi, lhs_lo, before, first, after):
                def body(n, before_, hooks):
                    product("A", ab0 + n, base, PJ, n, 0, 8, uT_hi, uT_lo, None, hooks)
                    product("B", ab0 + n, base, PJ, n, 8, 8, lhs_hi, lhs_lo, before_, hooks)
                body(0, before, first)
                with pe.Fori(1, DB) as n:
                    body(n, None, after(n - 1))

            def mg_T(n):
                def f():
                    pe.wait_ge(ev["B"], AB["pm"] + 1 + n)
                    fill("C", C_PM + n)
                    transpose("C", tok_block)
                return {2: [f]}
            gated(S_PRG, AB["prg"], yr_hi, yr_lo, {8: [lambda: pe.wait_ge(mx["yr_lo"], DB)]}, rg_tail(DB - 1),
                  lambda n: None)
            gated(S_PM, AB["pm"], ym_hi, ym_lo, {8: [lambda: pe.wait_ge(mx["ym_lo"], DB)]}, None, mg_T)
            project(S_WO, 8, 2, AB["wo"], C_WO, 8, mg_hi, mg_lo,
                    {0: [lambda: pe.wait_ge(ev["C"], C_PM + DB - 1)], 6: [lambda: pe.wait_ge(ev["C"], C_PM + DB)]},
                    mg_T(DB - 1))
            ffn(1, {2: [norm_T(2, DB - 1, C_WO + DB - 1)]})


_OUT = (1, 256, 2048)


def kernel(**inputs):
    import numpy as np
    import concourse.bacc as bacc
    from concourse import mybir
    from concourse.bass_utils import run_bass_kernel_spmd

    nc = bacc.Bacc("TRN2", target_bir_lowering=False, num_devices=1, dynamic_dma_scratch_size=128)
    arrays, ins = {}, {}
    for name, value in inputs.items():
        a = np.ascontiguousarray(value)
        arrays[f"in_{name}"] = a
        ins[name] = nc.dram_tensor(f"in_{name}", a.shape, mybir.dt.from_np(a.dtype), kind="ExternalInput").ap()
    out = nc.dram_tensor("out", _OUT, mybir.dt.float32, kind="ExternalOutput").ap()
    hybrid_block(nc, ins, out)
    return run_bass_kernel_spmd(nc, [arrays], core_ids=[0]).results[0]["out"]
```
